# Optimizing a Trainium2 kernel written in Bass

```python
import math
import jax, jax.numpy as jnp
from jax import lax
import numpy as np

D_MODEL = 1024
BATCH = 1
SEQ = 256
DEPTH = 2

HEAD_DIM = 64
ATT_HEADS = D_MODEL // HEAD_DIM
ATT_WIDTH = ATT_HEADS * HEAD_DIM
ROT_DIM = HEAD_DIM // 4
ROPE_THETA = 500000.0
DILATED_PATTERNS = ((128, 1), (512, 4), (2048, 16))
MAX_REACH = 2048
Q_BLOCK = 128
SSM_WIDTH = D_MODEL // 2
SSM_GROUP = 16
SSM_GROUPS = SSM_WIDTH // SSM_GROUP
SSM_STATE = 64
POOL_WIDTH = 2 * D_MODEL
POOL_WINDOWS = (2, 4, 8, 16)
POOL_GROUP = POOL_WIDTH // len(POOL_WINDOWS)
EVEN_IN = 4 * ATT_WIDTH + 2 * SSM_WIDTH
EVEN_OUT = ATT_WIDTH + SSM_WIDTH
ODD_IN = 2 * POOL_WIDTH
N_EVEN = (DEPTH + 1) // 2
N_ODD = DEPTH // 2
RMS_EPS = 1e-6


def rmsnorm(x, gain):
    xf = x.astype(jnp.float32)
    y = xf * lax.rsqrt(jnp.mean(xf * xf, axis=-1, keepdims=True) + RMS_EPS)
    return (y * gain.astype(jnp.float32)).astype(x.dtype)

def apply_partial_rope(x, pos):
    half = ROT_DIM // 2
    inv_freq = ROPE_THETA ** (-jnp.arange(0, ROT_DIM, 2, dtype=jnp.float32) / ROT_DIM)
    ang = pos.astype(jnp.float32)[:, None] * inv_freq[None, :]
    cos = jnp.cos(ang)[None, :, None, :]
    sin = jnp.sin(ang)[None, :, None, :]
    xr = x[..., :ROT_DIM].astype(jnp.float32)
    x1, x2 = xr[..., :half], xr[..., half:]
    rot = jnp.concatenate([x1 * cos - x2 * sin, x2 * cos + x1 * sin], axis=-1)
    return jnp.concatenate([rot.astype(x.dtype), x[..., ROT_DIM:]], axis=-1)

def dilated_offsets():
    return np.concatenate([np.arange(w // d + 1) * d for w, d in DILATED_PATTERNS]).astype(np.int32)

def dilated_attention(q, k, v):
    b, s, h, dh = q.shape
    offsets = jnp.asarray(dilated_offsets())
    qh = q.transpose(0, 2, 1, 3)
    pad = ((0, 0), (0, 0), (MAX_REACH, 0), (0, 0))
    k_pad = jnp.pad(k.transpose(0, 2, 1, 3), pad)
    v_pad = jnp.pad(v.transpose(0, 2, 1, 3), pad)

    def block(bi):
        start = bi * Q_BLOCK
        q_blk = lax.dynamic_slice_in_dim(qh, start, Q_BLOCK, axis=2)
        rel = start + jnp.arange(Q_BLOCK, dtype=jnp.int32)[:, None] - offsets[None, :]
        k_g = k_pad[:, :, rel + MAX_REACH]
        v_g = v_pad[:, :, rel + MAX_REACH]
        scores = jnp.einsum('bhqd,bhqkd->bhqk', q_blk, k_g).astype(jnp.float32)
        scores = jnp.where(rel >= 0, scores, -jnp.inf)
        p = jax.nn.softmax(scores, axis=-1)
        return jnp.einsum('bhqk,bhqkd->bhqd', p.astype(v.dtype), v_g)

    out = lax.map(block, jnp.arange(s // Q_BLOCK, dtype=jnp.int32))
    return out.transpose(1, 0, 3, 2, 4).reshape(b, s, h * dh)

def s5_ssm(u, a_re, a_im, log_dt, b_re, b_im, c_re, c_im, d_skip, glu_w, glu_b):
    bsz, s, _ = u.shape
    f32 = jnp.float32
    uf = u.astype(f32)
    ug = uf.reshape(bsz, s, SSM_GROUPS, SSM_GROUP)
    lam = lax.complex(a_re.astype(f32), a_im.astype(f32))
    dt = jnp.exp(log_dt.astype(f32))[:, None]
    lam_bar = jnp.exp(lam * dt)
    b_mat = lax.complex(b_re.astype(f32), b_im.astype(f32))
    b_bar = ((lam_bar - 1.0) / lam)[..., None] * b_mat
    bu = jnp.einsum('bsgh,gph->bsgp', ug.astype(jnp.complex64), b_bar)
    a_seq = jnp.broadcast_to(lam_bar, bu.shape)

    def combine(left, right):
        a_l, s_l = left
        a_r, s_r = right
        return a_r * a_l, a_r * s_l + s_r

    _, states = lax.associative_scan(combine, (a_seq, bu), axis=1)
    c_mat = lax.complex(c_re.astype(f32), c_im.astype(f32))
    y = jnp.real(jnp.einsum('bsgp,ghp->bsgh', states, c_mat)).reshape(bsz, s, SSM_WIDTH)
    y = jax.nn.gelu(y + d_skip.astype(f32) * uf)
    y = y * jax.nn.sigmoid(y @ glu_w.astype(f32) + glu_b.astype(f32))
    return y.astype(u.dtype)

def multiscale_pool(u, pool_w, pool_scale):
    bsz, s, _ = u.shape
    ug = u.astype(jnp.float32).reshape(bsz, s, len(POOL_WINDOWS), POOL_GROUP)
    count_base = jnp.arange(1, s + 1, dtype=jnp.float32)[None, :, None]
    outs = []
    for g, w in enumerate(POOL_WINDOWS):
        ch = ug[:, :, g]
        cs = jnp.cumsum(ch, axis=1)
        lagged = jnp.pad(cs, ((0, 0), (w, 0), (0, 0)))[:, :s]
        mean = (cs - lagged) / jnp.minimum(count_base, float(w))
        outs.append(mean - ch)
    mixed = jnp.stack(outs, axis=2)
    y = jnp.einsum('bsgc,gcd->bsgd', mixed, pool_w.astype(jnp.float32)).reshape(bsz, s, POOL_WIDTH)
    return (y * pool_scale.astype(jnp.float32)).astype(u.dtype)

def even_mixer(h, w_in, w_out, a_re, a_im, log_dt, b_re, b_im, c_re, c_im, d_skip, glu_w, glu_b):
    bsz, s, _ = h.shape
    proj = h @ w_in
    cuts = [ATT_WIDTH, 2 * ATT_WIDTH, 3 * ATT_WIDTH, 4 * ATT_WIDTH, 4 * ATT_WIDTH + SSM_WIDTH]
    q, k, v, g_att, u_ssm, g_ssm = jnp.split(proj, cuts, axis=-1)
    pos = jnp.arange(s, dtype=jnp.int32)
    q = apply_partial_rope(q.reshape(bsz, s, ATT_HEADS, HEAD_DIM), pos) * (HEAD_DIM ** -0.5)
    k = apply_partial_rope(k.reshape(bsz, s, ATT_HEADS, HEAD_DIM), pos)
    v = v.reshape(bsz, s, ATT_HEADS, HEAD_DIM)
    att = dilated_attention(q, k, v)
    ssm = s5_ssm(u_ssm, a_re, a_im, log_dt, b_re, b_im, c_re, c_im, d_skip, glu_w, glu_b)
    merged = jnp.concatenate([att * jax.nn.silu(g_att), ssm * jax.nn.silu(g_ssm)], axis=-1)
    return merged @ w_out

def odd_mixer(h, w_in, pool_w, pool_scale, w_out):
    u, gate = jnp.split(h @ w_in, [POOL_WIDTH], axis=-1)
    y = multiscale_pool(u, pool_w, pool_scale)
    return (y * jax.nn.silu(gate)) @ w_out

def first_inputs(seed: int = 0) -> dict:
    key = jax.random.key(seed)
    ks = jax.random.split(key, 24)
    f32 = jnp.float32

    def nrm(k, shape, scale):
        return jax.random.normal(k, shape, f32) * scale

    n_idx = jnp.arange(SSM_STATE, dtype=f32)
    return {
        "x": jax.random.normal(ks[0], (BATCH, SEQ, D_MODEL), f32),
        "pre_norm": 1.0 + nrm(ks[1], (DEPTH, D_MODEL), 0.1),
        "post_norm": 1.0 + nrm(ks[2], (DEPTH, D_MODEL), 0.1),
        "even_w_in": nrm(ks[3], (N_EVEN, D_MODEL, EVEN_IN), D_MODEL ** -0.5),
        "even_w_out": nrm(ks[4], (N_EVEN, EVEN_OUT, D_MODEL), EVEN_OUT ** -0.5),
        "ssm_a_re": -0.5 + nrm(ks[5], (N_EVEN, SSM_GROUPS, SSM_STATE), 0.01),
        "ssm_a_im": math.pi * n_idx + nrm(ks[6], (N_EVEN, SSM_GROUPS, SSM_STATE), 0.01),
        "ssm_log_dt": jax.random.uniform(ks[7], (N_EVEN, SSM_GROUPS), f32, math.log(1e-3), math.log(1e-1)),
        "ssm_b_re": nrm(ks[8], (N_EVEN, SSM_GROUPS, SSM_STATE, SSM_GROUP), (2 * SSM_GROUP) ** -0.5),
        "ssm_b_im": nrm(ks[9], (N_EVEN, SSM_GROUPS, SSM_STATE, SSM_GROUP), (2 * SSM_GROUP) ** -0.5),
        "ssm_c_re": nrm(ks[10], (N_EVEN, SSM_GROUPS, SSM_GROUP, SSM_STATE), (2 * SSM_STATE) ** -0.5),
        "ssm_c_im": nrm(ks[11], (N_EVEN, SSM_GROUPS, SSM_GROUP, SSM_STATE), (2 * SSM_STATE) ** -0.5),
        "ssm_d": nrm(ks[12], (N_EVEN, SSM_WIDTH), 1.0),
        "ssm_glu_w": nrm(ks[13], (N_EVEN, SSM_WIDTH, SSM_WIDTH), SSM_WIDTH ** -0.5),
        "ssm_glu_b": nrm(ks[14], (N_EVEN, SSM_WIDTH), 0.02),
        "odd_w_in": nrm(ks[15], (N_ODD, D_MODEL, ODD_IN), D_MODEL ** -0.5),
        "pool_w": nrm(ks[16], (N_ODD, len(POOL_WINDOWS), POOL_GROUP, POOL_GROUP), POOL_GROUP ** -0.5),
        "pool_scale": 1.0 + nrm(ks[17], (N_ODD, POOL_WIDTH), 0.1),
        "odd_w_out": nrm(ks[18], (N_ODD, POOL_WIDTH, D_MODEL), POOL_WIDTH ** -0.5),
    }

def first_block(x, pre_norm, post_norm, even_w_in, even_w_out, ssm_a_re, ssm_a_im, ssm_log_dt,
              ssm_b_re, ssm_b_im, ssm_c_re, ssm_c_im, ssm_d, ssm_glu_w, ssm_glu_b,
              odd_w_in, pool_w, pool_scale, odd_w_out):
    for layer in range(DEPTH):
        h = rmsnorm(x, pre_norm[layer])
        i = layer // 2
        if layer % 2 == 0:
            y = even_mixer(h, even_w_in[i], even_w_out[i], ssm_a_re[i], ssm_a_im[i], ssm_log_dt[i],
                           ssm_b_re[i], ssm_b_im[i], ssm_c_re[i], ssm_c_im[i], ssm_d[i],
                           ssm_glu_w[i], ssm_glu_b[i])
        else:
            y = odd_mixer(h, odd_w_in[i], pool_w[i], pool_scale[i], odd_w_out[i])
        x = x + rmsnorm(y, post_norm[layer])
    return x


RET_HEAD_DIM = 128
RET_WIDTH = D_MODEL // 2
RET_HEADS = RET_WIDTH // RET_HEAD_DIM
HGRN_HEAD_DIM = 128
HGRN_WIDTH = D_MODEL - RET_WIDTH
HGRN_HEADS = HGRN_WIDTH // HGRN_HEAD_DIM
MIX_WIDTH = RET_WIDTH + HGRN_WIDTH
IN_WIDTHS = [RET_WIDTH] * 4 + [HGRN_WIDTH] * 5
IN_COLS = sum(IN_WIDTHS)
RET_CHUNK = 128
HGRN_CHUNK = 64
ROPE_BASE = 10000.0
N_EXPERTS = 16
CAPACITY_FACTOR = 2
EXPERT_FF = 1024
NORM_EPS = 1e-6


def rms_normalize(x):
    xf = x.astype(jnp.float32)
    return (xf * lax.rsqrt(jnp.mean(xf * xf, axis=-1, keepdims=True) + NORM_EPS)).astype(x.dtype)

def rms_norm(x, g):
    return rms_normalize(x) * g.astype(x.dtype)

def to_heads(t, n_heads):
    b, s, _ = t.shape
    return t.reshape(b, s, n_heads, -1).transpose(0, 2, 1, 3)

def from_heads(t):
    b, h, s, d = t.shape
    return t.transpose(0, 2, 1, 3).reshape(b, s, h * d)

def to_chunks(t, chunk):
    b, h, s, d = t.shape
    return t.reshape(b, h, s // chunk, chunk, d).transpose(2, 0, 1, 3, 4)

def from_chunks(t):
    n, b, h, c, d = t.shape
    return t.transpose(1, 2, 0, 3, 4).reshape(b, h, n * c, d)

def rotary(x, pos):
    half = x.shape[-1] // 2
    inv_freq = ROPE_BASE ** (-jnp.arange(half, dtype=jnp.float32) / half)
    ang = pos.astype(jnp.float32)[:, None] * inv_freq[None, :]
    cos = jnp.cos(ang).astype(x.dtype)
    sin = jnp.sin(ang).astype(x.dtype)
    x1, x2 = x[..., :half], x[..., half:]
    return jnp.concatenate([x1 * cos - x2 * sin, x1 * sin + x2 * cos], axis=-1)

def retention_scan(q, k, v, log_gamma, include_diag):
    b, h, s, dk = q.shape
    dv = v.shape[-1]
    dt = q.dtype
    L = RET_CHUNK
    t = jnp.arange(L, dtype=jnp.float32)
    diff = t[:, None] - t[None, :]
    mask = (diff >= 0) if include_diag else (diff > 0)
    lg = log_gamma[:, None, None]
    intra_decay = jnp.where(mask, jnp.exp(lg * jnp.maximum(diff, 0.0)), 0.0).astype(dt)
    q_decay = jnp.exp(log_gamma[:, None] * (t + 1.0))[:, :, None].astype(dt)
    k_decay = jnp.exp(log_gamma[:, None] * (L - 1.0 - t))[:, :, None].astype(dt)
    chunk_decay = jnp.exp(log_gamma * L)[:, None, None].astype(dt)

    def step(state, inp):
        qc, kc, vc = inp
        scores = jnp.einsum('bhid,bhjd->bhij', qc, kc) * intra_decay
        out = (jnp.einsum('bhij,bhjv->bhiv', scores, vc)
               + jnp.einsum('bhid,bhdv->bhiv', qc * q_decay, state))
        state = chunk_decay * state + jnp.einsum('bhjd,bhjv->bhdv', kc * k_decay, vc)
        return state, out

    state0 = jnp.zeros((b, h, dk, dv), dt)
    _, out = lax.scan(step, state0, (to_chunks(q, L), to_chunks(k, L), to_chunks(v, L)))
    return from_chunks(out)

def hgrn2_scan(q, k, v, log_f):
    b, h, s, dk = q.shape
    dv = v.shape[-1]
    dt = q.dtype
    L = HGRN_CHUNK
    causal = jnp.tril(jnp.ones((L, L), dtype=bool))[:, :, None]

    def step(state, inp):
        qc, kc, vc, gc = inp
        cum = jnp.cumsum(gc, axis=2)
        rel = jnp.exp(jnp.where(causal, cum[:, :, :, None, :] - cum[:, :, None, :, :], -jnp.inf)).astype(dt)
        scores = jnp.einsum('bhtd,bhsd,bhtsd->bhts', qc, kc, rel)
        out = (jnp.einsum('bhts,bhsv->bhtv', scores, vc)
               + jnp.einsum('bhtd,bhdv->bhtv', qc * jnp.exp(cum).astype(dt), state))
        cum_end = cum[:, :, -1, :]
        k_to_end = kc * jnp.exp(cum_end[:, :, None, :] - cum).astype(dt)
        state = (jnp.exp(cum_end).astype(dt)[..., None] * state
                 + jnp.einsum('bhsd,bhsv->bhdv', k_to_end, vc))
        return state, out

    state0 = jnp.zeros((b, h, dk, dv), dt)
    _, out = lax.scan(step, state0, (to_chunks(q, L), to_chunks(k, L), to_chunks(v, L), to_chunks(log_f, L)))
    return from_chunks(out)

def flip_seq(t):
    return jnp.flip(t, axis=2)

def hybrid_mixer(xn, w_in, ret_g, hgrn_g, w_out, lb):
    b, s, _ = xn.shape
    dt = xn.dtype
    proj = xn @ w_in
    splits = np.cumsum(IN_WIDTHS)[:-1].tolist()
    rq, rk, rv, rg, hq, hf_fwd, hf_bwd, hi, hg = jnp.split(proj, splits, axis=-1)

    pos = jnp.arange(s)
    q = rotary(to_heads(rq, RET_HEADS), pos)
    k = rotary(to_heads(rk, RET_HEADS), pos) * (RET_HEAD_DIM ** -0.5)
    v = to_heads(rv, RET_HEADS)
    log_gamma = jnp.log1p(-(2.0 ** (-5.0 - jnp.arange(RET_HEADS, dtype=jnp.float32))))
    r_out = (retention_scan(q, k, v, log_gamma, True)
             + flip_seq(retention_scan(flip_seq(q), flip_seq(k), flip_seq(v), log_gamma, False)))
    r_out = from_heads(rms_normalize(r_out)) * ret_g.astype(dt) * jax.nn.silu(rg)

    q2 = jax.nn.silu(to_heads(hq, HGRN_HEADS)) * (HGRN_HEAD_DIM ** -0.5)
    v2 = to_heads(hi, HGRN_HEADS)

    def forget(z):
        z = z.astype(jnp.float32)
        if lb is None:
            return jax.nn.log_sigmoid(z), jax.nn.sigmoid(-z).astype(dt)
        lbh = lb.astype(jnp.float32).reshape(HGRN_HEADS, 1, HGRN_HEAD_DIM)
        f = lbh + (1.0 - lbh) * jax.nn.sigmoid(z)
        return jnp.log(f), ((1.0 - lbh) * jax.nn.sigmoid(-z)).astype(dt)

    logf_f, k_f = forget(to_heads(hf_fwd, HGRN_HEADS))
    logf_b, k_b = forget(to_heads(hf_bwd, HGRN_HEADS))
    h_out = (hgrn2_scan(q2, k_f, v2, logf_f)
             + flip_seq(hgrn2_scan(flip_seq(q2), flip_seq(k_b), flip_seq(v2), flip_seq(logf_b))))
    h_out = rms_norm(from_heads(h_out), hgrn_g) * jax.nn.silu(hg)

    return jnp.concatenate([r_out, h_out], axis=-1) @ w_out

def expert_choice_ffn(xn, w_router, w_gate, w_up, w_down):
    b, s, d = xn.shape
    cap = CAPACITY_FACTOR * s // N_EXPERTS
    affinity = jax.nn.softmax((xn @ w_router).astype(jnp.float32), axis=-1)
    gate, idx = lax.top_k(jnp.swapaxes(affinity, 1, 2), cap)
    xe = jax.vmap(lambda xb, ib: xb[ib])(xn, idx)
    hid = (jax.nn.silu(jnp.einsum('becd,edf->becf', xe, w_gate))
           * jnp.einsum('becd,edf->becf', xe, w_up))
    ye = jnp.einsum('becf,efd->becd', hid, w_down) * gate[..., None].astype(xn.dtype)
    return jax.vmap(lambda yb, ib: jnp.zeros((s, d), yb.dtype).at[ib.reshape(-1)].add(yb.reshape(-1, d)))(ye, idx)

def second_inputs(seed: int = 0) -> dict:
    key = jax.random.key(seed)
    ks = jax.random.split(key, 14)
    f32 = jnp.float32
    x = jax.random.normal(ks[0], (BATCH, SEQ, D_MODEL), f32)
    norm1_g = 1.0 + 0.02 * jax.random.normal(ks[1], (DEPTH, D_MODEL), f32)
    w_in = jax.random.normal(ks[2], (DEPTH, D_MODEL, IN_COLS), f32) * D_MODEL ** -0.5
    ret_norm_g = 1.0 + 0.02 * jax.random.normal(ks[3], (DEPTH, RET_WIDTH), f32)
    hgrn_norm_g = 1.0 + 0.02 * jax.random.normal(ks[4], (DEPTH, HGRN_WIDTH), f32)
    w_out = jax.random.normal(ks[5], (DEPTH, MIX_WIDTH, D_MODEL), f32) * MIX_WIDTH ** -0.5
    lower_bounds = 0.1 * jax.random.normal(ks[6], (DEPTH, HGRN_WIDTH), f32)
    norm2_g = 1.0 + 0.02 * jax.random.normal(ks[7], (DEPTH, D_MODEL), f32)
    w_router = jax.random.normal(ks[8], (DEPTH, D_MODEL, N_EXPERTS), f32) * D_MODEL ** -0.5
    w_gate = jax.random.normal(ks[9], (DEPTH, N_EXPERTS, D_MODEL, EXPERT_FF), f32) * D_MODEL ** -0.5
    w_up = jax.random.normal(ks[10], (DEPTH, N_EXPERTS, D_MODEL, EXPERT_FF), f32) * D_MODEL ** -0.5
    w_down = jax.random.normal(ks[11], (DEPTH, N_EXPERTS, EXPERT_FF, D_MODEL), f32) * EXPERT_FF ** -0.5
    final_norm_g = 1.0 + 0.02 * jax.random.normal(ks[12], (D_MODEL,), f32)
    return {"x": x, "norm1_g": norm1_g, "w_in": w_in, "ret_norm_g": ret_norm_g,
            "hgrn_norm_g": hgrn_norm_g, "w_out": w_out, "lower_bounds": lower_bounds,
            "norm2_g": norm2_g, "w_router": w_router, "w_gate": w_gate, "w_up": w_up,
            "w_down": w_down, "final_norm_g": final_norm_g}

def second_block(x, norm1_g, w_in, ret_norm_g, hgrn_norm_g, w_out, lower_bounds,
              norm2_g, w_router, w_gate, w_up, w_down, final_norm_g):
    lbs = jax.nn.softmax(lower_bounds.astype(jnp.float32), axis=0)
    lbs = jnp.cumsum(lbs, axis=0) - lbs[0]
    h = x
    for layer in range(DEPTH):
        lb = lbs[layer] if layer > 0 else None
        h = h + hybrid_mixer(rms_norm(h, norm1_g[layer]), w_in[layer], ret_norm_g[layer],
                             hgrn_norm_g[layer], w_out[layer], lb)
        h = h + expert_choice_ffn(rms_norm(h, norm2_g[layer]), w_router[layer],
                                  w_gate[layer], w_up[layer], w_down[layer])
    return rms_norm(h, final_norm_g)


def setup_inputs(seed=0):
    out = dict(first_inputs(seed))
    for name, value in second_inputs(seed + 1).items():
        if name != "x":
            out[name + "_2"] = value
    return out


def reference(
    x, pre_norm, post_norm, even_w_in, even_w_out, ssm_a_re, ssm_a_im, ssm_log_dt, ssm_b_re,
    ssm_b_im, ssm_c_re, ssm_c_im, ssm_d, ssm_glu_w, ssm_glu_b, odd_w_in, pool_w, pool_scale,
    odd_w_out, norm1_g_2, w_in_2, ret_norm_g_2, hgrn_norm_g_2, w_out_2, lower_bounds_2,
    norm2_g_2, w_router_2, w_gate_2, w_up_2, w_down_2, final_norm_g_2,
):
    x = first_block(
        x, pre_norm, post_norm, even_w_in, even_w_out, ssm_a_re, ssm_a_im, ssm_log_dt, ssm_b_re,
        ssm_b_im, ssm_c_re, ssm_c_im, ssm_d, ssm_glu_w, ssm_glu_b, odd_w_in, pool_w, pool_scale,
        odd_w_out,
    )
    return second_block(
        x, norm1_g_2, w_in_2, ret_norm_g_2, hgrn_norm_g_2, w_out_2, lower_bounds_2, norm2_g_2,
        w_router_2, w_gate_2, w_up_2, w_down_2, final_norm_g_2,
    )


_drawn_inputs = setup_inputs


def setup_inputs(seed=0):
    import zlib

    import numpy as np

    out = dict(_drawn_inputs(seed))
    spreads = {}
    factors = {'ssm_a_re': 8.0,
     'ssm_glu_b': 5.917,
     'norm1_g_2': 2.822,
     'ret_norm_g_2': 6.363,
     'hgrn_norm_g_2': 6.573,
     'lower_bounds_2': 8.0,
     'norm2_g_2': 4.292,
     'final_norm_g_2': 2.832}
    for name, (base, spread) in spreads.items():
        noise = np.random.default_rng([zlib.crc32(name.encode()), seed]).standard_normal(out[name].shape)
        drawn = base * np.exp(spread * noise) if base else spread * noise
        out[name] = __import__('jax').numpy.asarray(drawn.astype(out[name].dtype))
    for name, factor in factors.items():
        out[name] = (out[name] * factor).astype(out[name].dtype)
    return out
```

```python
from contextlib import ExitStack
import math

import numpy as np
import concourse.bass as bass
from concourse import mybir

F32 = mybir.dt.float32
U8 = mybir.dt.uint8
ALU = mybir.AluOpType
ACT = mybir.ActivationFunctionType
X = mybir.AxisListType.X

P = 128
S = 256
D = 1024
NT = S // P
DC = D // P
HEADS, HD = 16, 64
ROT = HD // 4
SSM_W, SSM_G, SSM_H, SSM_N = 512, 32, 16, 64
SSM_TILES = SSM_G * SSM_N // P
WINDOWS = (2, 4, 8, 16)
POOL_W = 2048
RH, RD = 4, 128
LEVELS = 8
NE, CAP, FF = 16, 32, 1024
EPS = 1e-6
RING = 6
SLOT = 4096
MASKED = -1e30
ROUND = 12582912.0
TURN = 6.283185

VEC = {}
_at = 0
for _name, _n in [("pre0", 8), ("pre1", 8), ("n1_0", 8), ("n1_1", 8), ("n2_0", 8), ("n2_1", 8),
                  ("n2p_0", 8), ("n2p_1", 8), ("ret_0", 4), ("hgrn_0", 4), ("ret_1", 4), ("hgrn_1", 4),
                  ("pscale", 16), ("glu_b", 4), ("ssm_d", 4), ("lb0", 4), ("lb1", 4),
                  ("a_re", 16), ("a_im", 16), ("log_dt", 16)]:
    VEC[_name] = (_at, _at + _n)
    _at += _n
NVEC = _at

CON = {}
_at = 0
for _name, _n in [("ident", P), ("attmask", 3 * P), ("rope_c", NT * 8), ("rope_s", NT * 8), ("time", S),
                  ("rot_c", NT * 64), ("rot_s", NT * 64), ("slots", CAP)]:
    CON[_name] = (_at, _at + _n)
    _at += _n
NCON = _at


def constants():
    con = np.zeros((P, NCON), np.float32)
    put = lambda name, a: con.__setitem__((slice(None), slice(*CON[name])), np.asarray(a, np.float32).reshape(P, -1))
    put("ident", np.eye(P))
    i, j = np.arange(S)[:, None], np.arange(S)[None, :]
    d = i - j
    mult = (d <= 128).astype(float) + ((d % 4 == 0) & (d <= 512)) + ((d % 16 == 0) & (d <= 2048))
    logm = np.where((d >= 0) & (mult > 0), np.log(np.maximum(mult, 1)), MASKED)
    put("attmask", np.concatenate([logm[:P, :P], logm[P:, :]], 1))
    pos = np.arange(S, dtype=np.float32)
    inv = (np.float32(500000.0) ** (-np.arange(0, ROT, 2, dtype=np.float32) / ROT)).astype(np.float32)
    ang = pos[:, None] * inv[None, :]
    tok = lambda a: a.reshape(NT, P, -1).transpose(1, 0, 2)
    put("rope_c", tok(np.cos(ang)))
    put("rope_s", tok(np.sin(ang)))
    put("time", np.broadcast_to(pos, (P, S)))
    inv = (np.float32(10000.0) ** (-np.arange(64, dtype=np.float32) / 64)).astype(np.float32)
    ang = pos[:, None] * inv[None, :]
    put("rot_c", tok(np.cos(ang)))
    put("rot_s", tok(np.sin(ang)))
    put("slots", np.broadcast_to(np.arange(CAP), (P, CAP)))
    pool = np.zeros((P, 4, 3 * P), np.float32)
    for w, win in enumerate(WINDOWS):
        m = ((d >= 0) & (d < win)) / np.minimum(i + 1.0, win) - (d == 0)
        mt = m.T
        pool[:, w, :S] = mt[:P]
        pool[:, w, S:] = mt[P:, P:]
    lg = np.log1p(-(2.0 ** (-5.0 - np.arange(RH))))
    dec = np.exp(lg[:, None, None] * np.abs(d)[None]) * RD ** -0.5
    decay = dec.reshape(RH, NT, P, S).transpose(2, 0, 1, 3).astype(np.float32)
    a, b = np.arange(P)[:, None], np.arange(P)[None, :]
    masks = np.zeros((P, LEVELS, P), np.float32)
    masks[:, 0] = a == b
    for l in range(1, LEVELS):
        h = 1 << (l - 1)
        masks[:, l] = (a // (2 * h) == b // (2 * h)) & (a // h != b // h)
    return con, pool.reshape(P, -1), decay.reshape(P, -1), masks.reshape(P, -1)


class Chain:

    def __init__(self, eng, sem):
        self.eng, self.sem, self.n = eng, sem, 0

    def go(self, ins):
        self.n += 1
        ins.then_inc(self.sem, 1)

    def settle(self):
        self.eng.wait_ge(self.sem, self.n)

    def link(self, ins):
        self.go(ins)
        self.settle()


def build(nc, a, out, upto=99):
    with ExitStack() as ctx:
        def sb(name, shape, dt=F32):
            return ctx.enter_context(nc.sbuf_tensor(name, shape, dt))

        def sem(name):
            return ctx.enter_context(nc.semaphore(name))

        ring = sb("ring", [P, RING, SLOT])
        x = sb("x", [P, NT, D])
        xs = sb("xs", [P, NT, D])
        xT = sb("xT", [P, DC, S])
        row = sb("row", [P, D])
        vec = sb("vec", [P, NVEC])
        con = sb("con", [P, NCON])
        ssq = sb("ssq", [P, NT])
        std = sb("std", [P, NT])
        rstd = sb("rstd", [P, NT])
        WORK = 17920
        work = sb("work", [P, WORK])
        DP = [ctx.enter_context(nc.psum_tensor(f"dense{i}", [P, 2, 512], F32)) for i in range(2)]
        WB = [ctx.enter_context(nc.psum_tensor(f"bank{i}", [P, 512], F32)) for i in range(4)]

        def vc(name, c=None):
            lo, hi = VEC[name]
            return vec[:, lo:hi] if c is None else vec[:, lo + c:lo + c + 1]

        def cn(name):
            lo, hi = CON[name]
            return con[:, lo:hi]

        ident = cn("ident")

        def area(at, pattern, **sizes):
            n = 1
            for v in sizes.values():
                n *= v
            assert at + n <= WORK, (at, n)
            return work[:, at:at + n].rearrange(pattern, **sizes)

        q_tok = area(0, "p (i n) -> p i n", i=NT, n=D)
        k_tok = area(2048, "p (i n) -> p i n", i=NT, n=D)
        v_tok = area(4096, "p (i n) -> p i n", i=NT, n=D)
        gaT = area(6144, "p (c s) -> p c s", c=8, s=S)
        uT = area(8192, "p (c s) -> p c s", c=4, s=S)
        gsT = area(9216, "p (c s) -> p c s", c=4, s=S)
        qT = area(10240, "p (c s) -> p c s", c=8, s=S)
        kT = area(12288, "p (c s) -> p c s", c=8, s=S)
        mT0 = q_tok.rearrange("p i n -> p (i n)").rearrange("p (c s) -> p c s", c=8)
        turns = area(10240, "p (f s) -> p f s", f=2, s=S)
        whole = area(10752, "p (f s) -> p f s", f=2, s=S)
        frac = [area(11264 + 512 * b, "p (f s) -> p f s", f=2, s=S) for b in range(2)]
        cs = [area(12288 + 512 * b, "p (f s) -> p f s", f=2, s=S) for b in range(2)]
        mulc = area(13312, "p (f s) -> p f s", f=2, s=S)
        muls = area(13824, "p (f s) -> p f s", f=2, s=S)
        drive = area(14336, "p (f s) -> p f s", f=2, s=S)
        scan = area(14848, "p (f s) -> p f s", f=2, s=S)
        state = [area(15360, "p (f s) -> p f s", f=2, s=S), xs[:, 0, 0:512].rearrange("p (f s) -> p f s", f=2)]
        bmat = area(15872, "p (c f n) -> p c f n", c=4, f=2, n=P)
        cmat = xs[:, 1, :].rearrange("p (f t m) -> p f t m", f=2, t=SSM_TILES)
        ceff = area(16896, "p (f t m) -> p f t m", f=2, t=SSM_TILES, m=32)
        small = sb("small", [P, 16, 16])
        rtmp = sb("rtmp", [P, 512])
        eps = sb("eps", [P, 1])
        yg = xT[:, 0:4, :]
        sg = xT[:, 4:8, :]
        esc = [area(14336 + 384 * b, "p (k n) -> p k n", k=3, n=P) for b in range(2)]
        escT = [area(15104 + 384 * b, "p (k n) -> p k n", k=3, n=P) for b in range(2)]
        nmax = area(15872, "p (h i) -> p h i", h=HEADS, i=NT)
        esum = area(15904, "p (h i) -> p h i", h=HEADS, i=NT)
        erec = area(15936, "p (h i) -> p h i", h=HEADS, i=NT)
        att = xs
        u_tok = area(0, "p (i n) -> p i n", i=NT, n=POOL_W)
        gT = area(4096, "p (c s) -> p c s", c=16, s=S)
        mixT = area(8192, "p (c s) -> p c s", c=16, s=S)
        poolm = area(12288, "p (w n) -> p w n", w=4, n=3 * P)

        rq_tok = area(0, "p (i n) -> p i n", i=NT, n=512)
        rk_tok = area(1024, "p (i n) -> p i n", i=NT, n=512)
        rv_tok = area(2048, "p (i n) -> p i n", i=NT, n=512)
        v2_tok = area(3072, "p (i n) -> p i n", i=NT, n=512)
        rgT = area(4096, "p (h s) -> p h s", h=RH, s=S)
        hgT = area(5120, "p (h s) -> p h s", h=RH, s=S)
        Q2_AT, K2_AT = 6144, 8192
        q2 = area(Q2_AT, "p (d n) -> p d n", d=2, n=RH * S)
        k2 = area(K2_AT, "p (d h s) -> p d h s", d=2, h=RH, s=S)
        qs = area(10240, "p (h s) -> p h s", h=RH, s=S)
        pairs = area(11264, "p (j h t) -> p j h t", j=NT, h=RH, t=P)
        cross = area(12288, "p (j h t) -> p j h t", j=NT, h=RH, t=P)
        DEC_AT = [13312, 15360, 16384, 16896, 17152, 17280, 17344]
        decays = area(13312, "p (d h s) -> p d h s", d=2, h=RH, s=S)
        kdiag = xs[:, 0, :].rearrange("p (h s) -> p h s", h=RH)
        decay = area(Q2_AT, "p (h i n) -> p h i n", h=RH, i=NT, n=S)
        rqT = area(K2_AT, "p (h s) -> p h s", h=RH, s=S)
        rkT = area(K2_AT + 1024, "p (h s) -> p h s", h=RH, s=S)
        rsc = [area(10240 + 512 * b, "p (i n) -> p i n", i=NT, n=S) for b in range(2)]
        mix = xs
        mT = area(0, "p (c s) -> p c s", c=8, s=S)
        xeT = area(0, "p (k c) -> p k c", k=DC, c=CAP)
        chosen = area(512, "p (i e c) -> p i e c", i=NT, e=NE, c=CAP)
        weighed = area(1536, "p (i e c) -> p i e c", i=NT, e=NE, c=CAP)
        wsel = area(2560, "p (i q c) -> p i q c", i=NT, q=4, c=CAP)
        csel = area(2816, "p (i c) -> p i c", i=NT, c=CAP)
        wselT = area(3072, "p (i s) -> p i s", i=NT, s=P)
        sgate = area(3328, "p (n) -> p n", n=256)
        hid = area(3584, "p (m b) -> p m b", m=P, b=2)
        hidT = area(3840, "p (b c) -> p b c", b=2, c=P)
        ye = area(4096, "p (n) -> p n", n=256)
        affT = area(4608, "p (s) -> p s", s=S)[0:NE]
        selT = area(4864, "p (s) -> p s", s=S)[0:NE]
        rankT = area(5120, "p (s) -> p s", s=S)[0:NE]
        top8 = area(5376, "p (n) -> p n", n=8)[0:NE]
        affe = area(5384, "p (i e) -> p i e", i=NT, e=NE)
        aff = area(5416, "p (i e) -> p i e", i=NT, e=NE)
        slot = area(5448, "p (i e) -> p i e", i=NT, e=NE)
        zeros = area(5504, "p (n) -> p n", n=P)
        stat = sb("stat", [P, 8, 8])
        ones = sb("ones", [P, 1])
        lbt = sb("lbt", [P, 3, RH])
        wr = sb("wr", [P, 2, DC, NE])
        masks = sb("masks", [P, LEVELS, P], U8)

        units = []

        def by_columns(w, rows, lo, n):
            return w[0:rows, lo:lo + n].rearrange("(k p) n -> p k n", p=P), rows // P, n

        def by_rows(w, k0, nk):
            return w[k0 * P:(k0 + nk) * P, :].rearrange("(k p) n -> p k n", p=P), nk, w.shape[1]

        wi = a["even_w_in"][0]
        for lo in (4096, 4608, 0, 512, 1024, 1536, 2048, 2560, 3072, 3584):
            units.append(by_columns(wi, D, lo, 512))
        units.append(by_columns(a["ssm_glu_w"][0], SSM_W, 0, 512))
        for k0 in (8, 0, 4):
            units.append(by_rows(a["even_w_out"][0], k0, 4))
        for n in range(8):
            units.append(by_columns(a["odd_w_in"][0], D, 512 * n, 512))
        for g in range(4):
            units.append(by_columns(a["pool_w"][0][g], 512, 0, 512))
        for k in range(4):
            units.append(by_rows(a["odd_w_out"][0], 4 * k, 4))
        FIRST2, OUT2, MOE = [], [], []
        for l in range(2):
            FIRST2.append(len(units))
            for lo in (2048, 2560, 3072, 3584, 0, 512, 1024, 1536, 4096):
                units.append(by_columns(a["w_in_2"][l], D, lo, 512))
            OUT2.append(len(units))
            for k in range(2):
                units.append(by_rows(a["w_out_2"][l], 4 * k, 4))
            MOE.append(len(units))
            units += [None] * (6 * NE)

        landed = [sem(f"landed{i}") for i in range(RING)]
        unit_done = sem("unit_done")

        def slot_of(u):
            _, k, n = units[u]
            return ring[:, u % RING, 0:k * n].rearrange("p (k n) -> p k n", k=k)

        small_in = sem("small_in")
        x_in = sem("x_in")
        bmat_in = sem("bmat_in")
        cmat_in = sem("cmat_in")
        pool_in = sem("pool_in")
        row_in = sem("row_in")
        row_used = sem("row_used")
        act_own, dve_own, pool_own = sem("act_own"), sem("dve_own"), sem("pool_own")
        x_ready = sem("x_ready")
        std_ready = sem("std_ready")
        xs_ready = sem("xs_ready")
        xt_ps = sem("xt_ps")
        xT_ready = sem("xT_ready")
        dense_out = sem("dense_out")
        eps_set = sem("eps_set")
        gated = sem("gated")
        pv_done = sem("pv_done")
        rope_done = sem("rope_done")
        frac_ready = sem("frac_ready")
        phi_ready = sem("phi_ready")
        cs_ready = sem("cs_ready")
        cs_used = sem("cs_used")
        bu_ps = sem("bu_ps")
        bu_used = sem("bu_used")
        state_ready = sem("state_ready")
        y_ps = sem("y_ps")
        yd_ready = sem("yd_ready")
        yg_ready = sem("yg_ready")
        ssm_done = sem("ssm_done")
        tiny = sem("tiny")
        tiny_v = sem("tiny_v")
        qk_ps = sem("qk_ps")
        qk_sb = sem("qk_sb")
        sc_ps = sem("sc_ps")
        sc_max = sem("sc_max")
        sc_exp = sem("sc_exp")
        et_ps = sem("et_ps")
        et_sb = sem("et_sb")
        o_sb = sem("o_sb")
        at_ps = sem("at_ps")
        at_sb = sem("at_sb")
        sq_ready = sem("sq_ready")
        out_sent = sem("out_sent")
        masks_in = sem("masks_in")
        masks_set = sem("masks_set")
        router_in = sem("router_in")
        decay_in = sem("decay_in")
        rot_done = sem("rot_done")
        lb_diff = sem("lb_diff")
        lb_sig = sem("lb_sig")
        lv_ready = sem("lv_ready")
        lv_ps = sem("lv_ps")
        lv_sb = sem("lv_sb")
        ho_ps = sem("ho_ps")
        rt_ps = sem("rt_ps")
        rt_sb = sem("rt_sb")
        rs_ps = sem("rs_ps")
        rs_sb = sem("rs_sb")
        rp_ps = sem("rp_ps")
        head_sq = sem("head_sq")
        head_std = sem("head_std")
        mix_tok = sem("mix_tok")
        gm_ps = sem("gm_ps")
        gm_sb = sem("gm_sb")
        lg_ps = sem("lg_ps")
        lg_max = sem("lg_max")
        lg_exp = sem("lg_exp")
        aff_sb = sem("aff_sb")
        aff_ps = sem("aff_ps")
        slot_sb = sem("slot_sb")
        slot_ps = sem("slot_ps")
        sel_ready = sem("sel_ready")
        zero_set = sem("zero_set")
        esel = sem("esel")
        ge_ps = sem("ge_ps")
        xe_sb = sem("xe_sb")
        gt_sb = sem("gt_sb")
        sg_sb = sem("sg_sb")
        hid_sb = sem("hid_sb")
        ht_ps = sem("ht_ps")
        ht_sb = sem("ht_sb")
        ye_sb = sem("ye_sb")
        sc_y = sem("sc_y")
        final_done = sem("final_done")

        mix_ps = sem("mix_ps")
        mix_sb = sem("mix_sb")

        def halves(t, half, right):
            return t.rearrange("p (m r n) -> p m r n", r=2, n=half)[:, :, int(right), :]

        block = ctx.enter_context(nc.Block())

        @block.sync
        def _(sp):
            sp.dma_start(x[:], a["x"][0].rearrange("(i p) n -> p i n", p=P)).then_inc(x_in, 16)
            def load(u):
                src, k, n = units[u]
                if u >= RING:
                    sp.wait_ge(unit_done, u - RING + 1)
                sp.dma_start(slot_of(u), src).then_inc(landed[u % RING], 16)

            for u in range(FIRST2[0]):
                load(u)
            for l in range(2):
                for u in range(FIRST2[l], MOE[l]):
                    load(u)
                halves = [a[n][l].rearrange("e (p k) n -> e p k n", k=DC) for n in ("w_gate_2", "w_up_2")]
                down = a["w_down_2"][l].rearrange("e (q p b) n -> e p q b n", p=P, b=2)
                with sp.Fori(0, NE) as e:
                    for j in range(6):
                        s = (MOE[l] + j) % RING
                        sp.wait_ge(unit_done, e * 6 + (MOE[l] + j - RING + 1))
                        if j < 4:
                            src = halves[j % 2][bass.ds(e, 1), :, 4 * (j // 2):4 * (j // 2) + 4, :]
                            src, dst = src.rearrange("o p k n -> (o p) k n"), ring[:, s, :].rearrange("p (k n) -> p k n", k=4)
                        else:
                            src = down[bass.ds(e, 1), :, 2 * (j - 4):2 * (j - 4) + 2, :, :]
                            src = src.rearrange("o p q b n -> (o p) q (b n)")
                            dst = ring[:, s, :].rearrange("p (q n) -> p q n", q=2)
                        sp.dma_start(dst, src).then_inc(landed[s], 16)
            sp.wait_ge(final_done, NT)
            sp.dma_start(out.rearrange("(i p) n -> p i n", p=P), xs[:]).then_inc(out_sent, 16)
            sp.wait_ge(out_sent, 16)

        @block.gpsimd
        def _(gp):
            own = Chain(gp, pool_own)
            g = nc.gpsimd
            gp.dma_start(bmat, a["ssm_b"].rearrange("p (c f n) -> p c f n", c=4, f=2)).then_inc(bmat_in, 16)
            gp.dma_start(row[:], a["post_norm"][0:1, :].partition_broadcast(P)).then_inc(row_in, 16)
            gp.wait_ge(xt_ps, 4)
            gp.dma_start(cmat, a["ssm_c"].rearrange("p (f t m) -> p f t m", f=2, t=SSM_TILES)).then_inc(cmat_in, 16)
            gp.wait_ge(small_in, 32)
            gp.wait_ge(phi_ready, 1)
            for i in range(SSM_TILES):
                own.link(g.tensor_scalar(turns[:, 1, :], cn("time"), small[:, 0, i:i + 1], None, ALU.mult))
                own.link(g.tensor_scalar(turns[:, 0, :], turns[:, 1, :], 0.25, None, ALU.add))
                own.link(g.tensor_scalar(whole, turns, ROUND, None, ALU.add))
                own.link(g.tensor_scalar(whole, whole, -ROUND, None, ALU.add))
                if i >= 2:
                    gp.wait_ge(cs_ready, i - 1)
                g.tensor_tensor(frac[i % 2], turns, whole, ALU.subtract).then_inc(frac_ready, 1)
                gp.wait_ge(frac_ready, i + 1)
            for w, t in enumerate((q_tok, k_tok)):
                gp.wait_ge(dense_out, 4 + 2 * w)
                hv = t.rearrange("p i (h c) -> p i h c", c=HD)
                for i in range(NT):
                    x1, x2 = hv[:, i, :, 0:8], hv[:, i, :, 8:16]
                    cc = cn("rope_c").rearrange("p (i c) -> p i c", i=NT)[:, i:i + 1, :].to_broadcast([P, HEADS, 8])
                    ss = cn("rope_s").rearrange("p (i c) -> p i c", i=NT)[:, i:i + 1, :].to_broadcast([P, HEADS, 8])
                    t4 = [rtmp[:, n * P:(n + 1) * P].rearrange("p (h c) -> p h c", c=8) for n in range(4)]
                    own.go(g.tensor_tensor(t4[0], x1, cc, ALU.mult))
                    own.go(g.tensor_tensor(t4[1], x2, ss, ALU.mult))
                    own.go(g.tensor_tensor(t4[2], x2, cc, ALU.mult))
                    own.link(g.tensor_tensor(t4[3], x1, ss, ALU.mult))
                    g.tensor_tensor(x1, t4[0], t4[1], ALU.subtract).then_inc(rope_done, 1)
                    g.tensor_tensor(x2, t4[2], t4[3], ALU.add).then_inc(rope_done, 1)
                    gp.wait_ge(rope_done, 4 * w + 2 * i + 2)
            gp.wait_ge(pv_done, HEADS)
            gp.dma_start(poolm, a["pool_mat"].rearrange("p (w n) -> p w n", w=4)).then_inc(pool_in, 16)
            gp.wait_ge(x_ready, 2)
            gp.dma_start(row[:], a["post_norm"][1:2, :].partition_broadcast(P)).then_inc(row_in, 16)
            gp.wait_ge(x_ready, 4)
            n_rot = 0
            for l in range(2):
                for w, t in enumerate((rq_tok, rk_tok)):
                    gp.wait_ge(dense_out, 26 + 11 * l + 7 + w)
                    hv = t.rearrange("p i (h c) -> p i h c", c=RD)
                    for i in range(NT):
                        x1, x2 = hv[:, i, :, 0:64], hv[:, i, :, 64:128]
                        cc = cn("rot_c").rearrange("p (i c) -> p i c", i=NT)[:, i:i + 1, :].to_broadcast([P, RH, 64])
                        ss = cn("rot_s").rearrange("p (i c) -> p i c", i=NT)[:, i:i + 1, :].to_broadcast([P, RH, 64])
                        t4 = [row[:, n * 256:(n + 1) * 256].rearrange("p (h c) -> p h c", c=64) for n in range(4)]
                        own.go(g.tensor_tensor(t4[0], x1, cc, ALU.mult))
                        own.go(g.tensor_tensor(t4[1], x2, ss, ALU.mult))
                        own.go(g.tensor_tensor(t4[2], x2, cc, ALU.mult))
                        own.link(g.tensor_tensor(t4[3], x1, ss, ALU.mult))
                        g.tensor_tensor(x1, t4[0], t4[1], ALU.subtract).then_inc(rot_done, 1)
                        g.tensor_tensor(x2, t4[2], t4[3], ALU.add).then_inc(rot_done, 1)
                        n_rot += 2
                        gp.wait_ge(rot_done, n_rot)
                gp.wait_ge(lv_ps, 9 * (l + 1))
                gp.dma_start(decay.rearrange("p h i n -> p (h i n)"), a["decay"]).then_inc(decay_in, 16)
                gp.wait_ge(sel_ready, 2 * (l + 1))
                with gp.Fori(0, NE) as e:
                    gp.wait_ge(ge_ps, e + ((NE + 1) * l + 1))
                    ch = chosen.rearrange("p i e c -> p i (e c)")[:, :, bass.ds(e * CAP, CAP)]
                    g.tensor_copy(csel, ch).then_inc(esel, 1)
                    for i in range(NT):
                        we = weighed.rearrange("p i e c -> p i (e c)")[:, i:i + 1, bass.ds(e * CAP, CAP)]
                        g.tensor_copy(wsel[:, i], we.to_broadcast([P, 4, CAP])).then_inc(esel, 1)
            gp.wait_ge(rot_done, n_rot)
            gp.dma_start(row[:], a["final_norm_g_2"].rearrange("(o n) -> o n", o=1).partition_broadcast(P)).then_inc(row_in, 16)

        @block.scalar
        def _(act):
            own = Chain(act, act_own)
            s = nc.scalar
            act.dma_start(vec[:], a["vectors"]).then_inc(small_in, 16)
            act.dma_start(con[:], a["constants"]).then_inc(small_in, 16)
            act.dma_start(xT[:, 0:4, :], a["pair_masks"].rearrange("p (c n) -> p c n", c=4)).then_inc(masks_in, 16)
            for l in range(2):
                act.dma_start(wr[:, l], a["w_router_2"][l].rearrange("(k p) e -> p k e", p=P)).then_inc(router_in, 16)

            def rms(n, src):
                for i in range(NT):
                    s.activation(xs[:, i, :], src(i), ACT.Square, accum_out=ssq[:, i:i + 1]).then_inc(sq_ready, 1)
                    act.wait_ge(sq_ready, 2 * n + i + 1)
                s.activation(std[:], ssq[:], ACT.Sqrt, scale=1.0 / D, bias=eps[:]).then_inc(std_ready, 1)

            def tok_out(u, dst, lo, scale=1.0):
                act.wait_ge(unit_done, u + 1)
                s.activation(dst[:, :, lo:lo + 512], DP[u % 2][:], ACT.Copy, scale=scale).then_inc(dense_out, 1)

            def t_out(u, dst, c0, func=ACT.Copy):
                act.wait_ge(unit_done, u + 1)
                s.activation(dst[:, c0:c0 + 4, :], DP[u % 2][:].rearrange("p b (c s) -> p (b c) s", c=2),
                             func).then_inc(dense_out, 1)

            act.wait_ge(small_in, 32)
            s.activation(small[:, 1, :], vc("log_dt"), ACT.Exp).then_inc(tiny, 1)
            act.wait_ge(tiny, 1)
            s.activation(small[:, 2, :], small[:, 1, :], ACT.Ln).then_inc(tiny, 1)
            act.wait_ge(tiny_v, 1)
            s.activation(small[:, 5, :], small[:, 4, :], ACT.Exp).then_inc(tiny, 1)
            act.wait_ge(tiny, 3)
            s.activation(small[:, 6, :], small[:, 5, :], ACT.Ln).then_inc(tiny, 1)
            act.wait_ge(x_in, 16)
            act.wait_ge(eps_set, 1)
            rms(0, lambda i: x[:, i, :])
            act.wait_ge(tiny_v, 2)
            s.activation(small[:, 8:10, :], small[:, 8:10, :], ACT.Sin, scale=TURN).then_inc(tiny, 1)

            def sincos(i):
                act.wait_ge(frac_ready, i + 1)
                if i >= 2:
                    act.wait_ge(cs_used, i - 1)
                s.activation(cs[i % 2], frac[i % 2], ACT.Sin, scale=TURN).then_inc(cs_ready, 1)

            t_out(0, uT, 0)
            t_out(1, gsT, 0, ACT.Silu)
            for m in range(2, 10):
                sincos(2 * (m - 2))
                sincos(2 * (m - 2) + 1)
                if m < 4:
                    tok_out(m, q_tok, 512 * (m - 2), HD ** -0.5)
                elif m < 6:
                    tok_out(m, k_tok, 512 * (m - 4))
                elif m < 8:
                    tok_out(m, v_tok, 512 * (m - 6))
                else:
                    t_out(m, gaT, 4 * (m - 8), ACT.Silu)
            for c in range(4):
                act.wait_ge(yd_ready, c + 1)
                s.activation(yg[:, c, :], uT[:, c, :], ACT.Gelu_apprx_tanh).then_inc(yg_ready, 1)
            act.wait_ge(unit_done, 11)
            for c in range(4):
                s.activation(sg[:, c, :], DP[0][:, c // 2, (c % 2) * S:(c % 2 + 1) * S], ACT.Sigmoid,
                             bias=vc("glu_b", c)).then_inc(dense_out, 1)
            for b in range(8):
                act.wait_ge(qk_ps, b + 1)
                dst = (qT if b < 4 else kT)[:, 2 * (b % 4):2 * (b % 4) + 2, :]
                s.activation(dst, WB[b % 4][:].rearrange("p (c s) -> p c s", c=2), ACT.Copy).then_inc(qk_sb, 1)
            for h in range(HEADS):
                act.wait_ge(sc_max, 2 * h + 2)
                s.activation(esc[h % 2][:, 0:1, :], esc[h % 2][:, 0:1, :], ACT.Exp, scale=-1.0,
                             bias=nmax[:, h, 0:1], accum_out=esum[:, h, 0:1]).then_inc(sc_exp, 1)
                s.activation(esc[h % 2][:, 1:3, :], esc[h % 2][:, 1:3, :], ACT.Exp, scale=-1.0,
                             bias=nmax[:, h, 1:2], accum_out=esum[:, h, 1:2]).then_inc(sc_exp, 1)
            act.wait_ge(unit_done, 14)
            rms(1, lambda i: DP[i][:].rearrange("p a b -> p (a b)"))
            act.wait_ge(x_ready, 2)
            rms(2, lambda i: x[:, i, :])
            for g in range(4):
                tok_out(14 + g, u_tok, 512 * g)
                for b in range(2):
                    act.wait_ge(mix_ps, 2 * g + b + 1)
                    s.activation(mixT[:, 4 * g + 2 * b:4 * g + 2 * b + 2, :],
                                 WB[(2 * g + b) % 4][:].rearrange("p (c s) -> p c s", c=2), ACT.Copy).then_inc(mix_sb, 1)
            for g in range(4):
                t_out(18 + g, gT, 4 * g, ACT.Silu)
            act.wait_ge(unit_done, 30)
            rms(3, lambda i: DP[i][:].rearrange("p a b -> p (a b)"))

            act.wait_ge(lb_diff, 1)
            s.activation(lbt[:, 1, :], lbt[:, 0, :], ACT.Sigmoid).then_inc(lb_sig, 1)
            s.activation(lbt[:, 2, :], lbt[:, 0, :], ACT.Sigmoid, scale=-1.0).then_inc(lb_sig, 1)
            for l in range(2):
                u = FIRST2[l]
                act.wait_ge(x_ready, 4 + 6 * l)
                rms(4 + 2 * l, lambda i: x[:, i, :])
                t_out(u, qs, 0, ACT.Silu)
                for d in range(2):
                    act.wait_ge(unit_done, u + d + 2)
                    z = DP[(u + 1 + d) % 2][:].rearrange("p b (c s) -> p (b c) s", c=2)
                    s.activation(decays[:, 1 - d], z, ACT.Sigmoid).then_inc(dense_out, 1)
                    s.activation(k2[:, d], z, ACT.Sigmoid, scale=-1.0).then_inc(dense_out, 1)
                for n, t in enumerate((v2_tok, rq_tok, rk_tok, rv_tok)):
                    tok_out(u + 3 + n, t, 0)
                t_out(u + 7, rgT, 0, ACT.Silu)
                t_out(u + 8, hgT, 0, ACT.Silu)
                act.wait_ge(ho_ps, l + 1)
                for j in range(NT):
                    s.activation(rtmp[:], WB[2 + j][:], ACT.Square, accum_out=stat[:, 0, j:j + 1]).then_inc(head_sq, 1)
                    act.wait_ge(head_sq, 10 * l + j + 1)
                s.activation(stat[:, 1, 0:2], stat[:, 0, 0:2], ACT.Sqrt, scale=1.0 / 512, bias=eps[:]).then_inc(head_std, 1)
                for w, t in enumerate((rqT, rkT)):
                    act.wait_ge(rt_ps, 2 * l + w + 1)
                    s.activation(t, DP[w][:].rearrange("p b (c s) -> p (b c) s", c=2), ACT.Copy).then_inc(rt_sb, 1)
                act.wait_ge(rp_ps, RH * (l + 1))
                for j in range(NT):
                    for h in range(RH):
                        s.activation(rtmp[:, 0:P], DP[0][:, j, h * P:(h + 1) * P], ACT.Square,
                                     accum_out=stat[:, 2, 4 * j + h:4 * j + h + 1]).then_inc(head_sq, 1)
                        act.wait_ge(head_sq, 10 * l + 2 + 4 * j + h + 1)
                s.activation(stat[:, 3, :], stat[:, 2, :], ACT.Sqrt, scale=1.0 / RD, bias=eps[:]).then_inc(head_std, 1)
                act.wait_ge(x_ready, 6 + 6 * l)
                rms(5 + 2 * l, lambda i: x[:, i, :])
                act.wait_ge(lg_max, l + 1)
                for i in range(NT):
                    s.activation(affe[:, i, :], WB[0][:, NE * i:NE * i + NE], ACT.Exp, bias=stat[:, 5, i:i + 1],
                                 accum_out=stat[:, 6, i:i + 1]).then_inc(lg_exp, 1)
                with act.Fori(0, NE) as e:
                    act.wait_ge(xe_sb, e + (NE * l + 1))
                    s.activation(wselT, WB[1][:, 256:512].rearrange("p (i s) -> p i s", i=NT), ACT.Copy).then_inc(gt_sb, 1)
                    act.wait_ge(unit_done, e * 6 + (MOE[l] + 4))
                    s.activation(sgate, WB[0][:, 0:256], ACT.Silu).then_inc(sg_sb, 1)
                    act.wait_ge(ht_ps, e + (NE * l + 1))
                    s.activation(hidT, WB[2][:, 0:256].rearrange("p (b c) -> p b c", b=2), ACT.Copy).then_inc(ht_sb, 1)
            act.wait_ge(x_ready, 16)
            rms(8, lambda i: x[:, i, :])

        @block.vector
        def _(dve):
            own = Chain(dve, dve_own)
            v = nc.vector
            tt, ts, stt = v.tensor_tensor, v.tensor_scalar, v.scalar_tensor_tensor
            v.memset(eps[:], EPS).then_inc(eps_set, 1)
            dve.wait_ge(masks_in, 16)
            v.tensor_copy(masks[:].rearrange("p l n -> p (l n)"), xT[:, 0:4, :].rearrange("p c s -> p (c s)")).then_inc(masks_set, 1)
            dve.wait_ge(masks_set, 1)
            dve.wait_ge(small_in, 32)

            def sm(n):
                return small[:, n, :]
            dve.wait_ge(tiny, 2)
            own.link(tt(sm(3), vc("log_dt"), sm(2), ALU.subtract))
            own.link(stt(sm(3), sm(3), 1.0, sm(1), ALU.add, ALU.mult))
            tt(sm(4), vc("a_re"), sm(3), ALU.mult).then_inc(tiny_v, 1)
            own.link(tt(sm(7), vc("a_im"), sm(3), ALU.mult))
            own.link(ts(sm(10), sm(7), 1.0 / (2 * math.pi), None, ALU.mult))
            own.link(ts(sm(11), sm(10), ROUND, None, ALU.add))
            own.link(ts(sm(11), sm(11), -ROUND, None, ALU.add))
            own.link(stt(sm(12), sm(11), -6.28125, sm(7), ALU.mult, ALU.add))
            own.link(stt(sm(12), sm(11), -(2 * math.pi - 6.28125), sm(12), ALU.mult, ALU.add))
            ts(sm(0), sm(12), 1.0 / (2 * math.pi), None, ALU.mult).then_inc(phi_ready, 1)
            dve.wait_ge(phi_ready, 1)
            own.link(ts(sm(8), sm(0), 0.25, None, ALU.add))
            own.go(ts(sm(10), sm(8), ROUND, None, ALU.add))
            own.link(ts(sm(11), sm(0), ROUND, None, ALU.add))
            own.link(ts(small[:, 10:12, :], small[:, 10:12, :], -ROUND, None, ALU.add))
            own.link(tt(sm(8), sm(8), sm(10), ALU.subtract))
            tt(sm(9), sm(0), sm(11), ALU.subtract).then_inc(tiny_v, 1)
            dve.wait_ge(tiny, 4)
            own.link(tt(sm(6), sm(4), sm(6), ALU.subtract))
            own.link(stt(sm(5), sm(6), 1.0, sm(5), ALU.add, ALU.mult))

            def normalise(n, k):
                dve.wait_ge(std_ready, n + 1)
                own.link(v.reciprocal(rstd[:], std[:]))
                for i in range(NT):
                    ts(xs[:, i, :], x[:, i, :], rstd[:, i:i + 1], None, ALU.mult).then_inc(xs_ready, 1)

            def gain_out(k, name):
                for b in range(4):
                    i, half = b // 2, b % 2
                    dve.wait_ge(xt_ps, 4 * k + b + 1)
                    g = vc(name)[:, 4 * half:4 * half + 4].unsqueeze(2).to_broadcast([P, 4, P])
                    tt(xT[:, 4 * half:4 * half + 4, i * P:(i + 1) * P], WB[b][:].rearrange("p (c s) -> p c s", c=4),
                       g, ALU.mult).then_inc(xT_ready, 1)

            def post_norm(n, k):
                dve.wait_ge(std_ready, n + 1)
                dve.wait_ge(row_in, 16 * (k + 1))
                own.link(v.reciprocal(rstd[:], std[:]))
                for i in range(NT):
                    stt(xT[:, 4 * i:4 * i + 4, :].rearrange("p c s -> p (c s)"), DP[i][:].rearrange("p b n -> p (b n)"),
                        rstd[:, i:i + 1], row[:], ALU.mult, ALU.mult).then_inc(dense_out, 1)
                own.settle()

            normalise(0, 0)
            dve.wait_ge(xs_ready, 2)
            dve.wait_ge(tiny, 5)
            dve.wait_ge(cmat_in, 16)
            own.go(tt(sm(1), sm(5), sm(8), ALU.mult))
            own.link(tt(sm(2), sm(5), sm(9), ALU.mult))
            own.go(ts(sm(1), sm(1), -1.0, None, ALU.add))
            own.go(tt(sm(10), vc("a_re"), vc("a_re"), ALU.mult))
            own.link(tt(sm(11), vc("a_im"), vc("a_im"), ALU.mult))
            own.link(tt(sm(10), sm(10), sm(11), ALU.add))
            own.link(v.reciprocal(sm(10), sm(10)))
            own.go(tt(sm(11), sm(1), vc("a_re"), ALU.mult))
            own.go(tt(sm(12), sm(2), vc("a_im"), ALU.mult))
            own.go(tt(sm(13), sm(2), vc("a_re"), ALU.mult))
            own.link(tt(sm(14), sm(1), vc("a_im"), ALU.mult))
            own.go(tt(sm(11), sm(11), sm(12), ALU.add))
            own.link(tt(sm(13), sm(13), sm(14), ALU.subtract))
            own.go(tt(sm(11), sm(11), sm(10), ALU.mult))
            own.link(tt(sm(13), sm(13), sm(10), ALU.mult))
            gain_out(0, "pre0")
            kr = sm(11).unsqueeze(2).to_broadcast([P, 16, 32])
            ki = sm(13).unsqueeze(2).to_broadcast([P, 16, 32])
            t1 = mulc.rearrange("p f s -> p (f s)").rearrange("p (t m) -> p t m", t=16)
            t2 = muls.rearrange("p f s -> p (f s)").rearrange("p (t m) -> p t m", t=16)
            own.go(tt(t1, cmat[:, 0], kr, ALU.mult))
            own.link(tt(t2, cmat[:, 1], ki, ALU.mult))
            own.link(tt(ceff[:, 0], t1, t2, ALU.subtract))
            own.go(tt(t1, cmat[:, 0], ki, ALU.mult))
            own.link(tt(t2, cmat[:, 1], kr, ALU.mult))
            own.link(stt(ceff[:, 1], t1, -1.0, t2, ALU.mult, ALU.subtract))
            for i in range(SSM_TILES):
                cosb = cs[i % 2][:, 0:1, :].to_broadcast([P, 2, S])
                sinb = cs[i % 2][:, 1:2, :].to_broadcast([P, 2, S])
                bu = WB[i % 2][:].rearrange("p (f s) -> p f s", f=2)
                dve.wait_ge(cs_ready, i + 1)
                dve.wait_ge(bu_ps, i + 1)
                own.go(tt(mulc, bu, cosb, ALU.mult))
                tt(muls, bu, sinb, ALU.mult).then_inc(bu_used, 1)
                own.settle()
                dve.wait_ge(bu_used, i + 1)
                own.go(tt(drive[:, 0, :], mulc[:, 0, :], muls[:, 1, :], ALU.add))
                own.link(tt(drive[:, 1, :], mulc[:, 1, :], muls[:, 0, :], ALU.subtract))
                r = small[:, 5, i:i + 1].to_broadcast([P, S])
                for f in range(2):
                    own.go(v.tensor_tensor_scan(scan[:, f, :], r, drive[:, f, :], 0.0, ALU.mult, ALU.add))
                own.settle()
                own.go(tt(mulc, scan, cosb, ALU.mult))
                tt(muls, scan, sinb, ALU.mult).then_inc(cs_used, 1)
                own.settle()
                dve.wait_ge(cs_used, i + 1)
                if i >= 2:
                    dve.wait_ge(y_ps, i - 1)
                tt(state[i % 2][:, 0, :], mulc[:, 0, :], muls[:, 1, :], ALU.subtract).then_inc(state_ready, 1)
                tt(state[i % 2][:, 1, :], mulc[:, 1, :], muls[:, 0, :], ALU.add).then_inc(state_ready, 1)
                dve.wait_ge(state_ready, 2 * i + 2)
                if i % 4 == 3:
                    c = i // 4
                    dve.wait_ge(y_ps, i + 1)
                    stt(uT[:, c, :], uT[:, c, :], vc("ssm_d", c), WB[2 + c % 2][:, 0:S], ALU.mult,
                        ALU.add).then_inc(yd_ready, 1)
            dve.wait_ge(dense_out, 14)
            own.link(tt(sg, sg, yg, ALU.mult))
            tt(gsT, gsT, sg, ALU.mult).then_inc(ssm_done, 1)

            def spread_heads(hb):
                dve.wait_ge(pv_done, 4 * hb + 4)
                own.link(v.reciprocal(erec[:, 4 * hb:4 * hb + 4, :], esum[:, 4 * hb:4 * hb + 4, :]))
                for i in range(NT):
                    src = WB[3][:].rearrange("p (h i n) -> p i h n", h=4, i=NT)[:, i]
                    rec = erec[:, 4 * hb:4 * hb + 4, i:i + 1].to_broadcast([P, 4, HD])
                    tt(att[:, i, 256 * hb:256 * hb + 256].rearrange("p (h n) -> p h n", h=4), src, rec,
                       ALU.mult).then_inc(o_sb, 1)

            am = cn("attmask")
            for h in range(HEADS + 1):
                if h < HEADS:
                    dve.wait_ge(sc_ps, h + 1)
                    if h >= 2:
                        dve.wait_ge(et_ps, h - 1)
                    v.tensor_tensor_reduce(esc[h % 2][:, 0, :], WB[h % 2][:, 0:P], am[:, 0:P], -1.0, -MASKED,
                                           ALU.add, ALU.min, nmax[:, h, 0:1]).then_inc(sc_max, 1)
                    v.tensor_tensor_reduce(esc[h % 2][:, 1:3, :].rearrange("p k n -> p (k n)"), WB[h % 2][:, P:3 * P],
                                           am[:, P:3 * P], -1.0, -MASKED, ALU.add, ALU.min,
                                           nmax[:, h, 1:2]).then_inc(sc_max, 1)
                if h >= 1:
                    dve.wait_ge(et_ps, h)
                    if h >= 3:
                        dve.wait_ge(pv_done, h - 2)
                    v.tensor_copy(escT[(h - 1) % 2].rearrange("p k n -> p (k n)"),
                                  WB[2][:, 0:3 * P]).then_inc(et_sb, 1)
                if h >= 5 and (h - 5) % 4 == 0:
                    spread_heads((h - 5) // 4)
            spread_heads(3)
            for b in range(4):
                dve.wait_ge(at_ps, b + 1)
                tt(mT0[:, 2 * b:2 * b + 2, :], WB[b][:].rearrange("p (c s) -> p c s", c=2),
                   gaT[:, 2 * b:2 * b + 2, :], ALU.mult).then_inc(at_sb, 1)
            post_norm(1, 0)
            dve.wait_ge(dense_out, 16)
            for i in range(NT):
                tt(x[:, i, :], x[:, i, :], xT[:, 4 * i:4 * i + 4, :].rearrange("p c s -> p (c s)"),
                   ALU.add).then_inc(x_ready, 1)
            dve.wait_ge(x_ready, 2)
            normalise(2, 1)
            gain_out(1, "pre1")
            for g in range(4):
                dve.wait_ge(unit_done, 23 + g)
                d = DP[g % 2]
                for c in range(4):
                    ins = stt(gT[:, 4 * g + c, :], d[:, c // 2, (c % 2) * S:(c % 2 + 1) * S], vc("pscale", 4 * g + c),
                              gT[:, 4 * g + c, :], ALU.mult, ALU.mult).then_inc(gated, 1)
            post_norm(3, 1)
            dve.wait_ge(dense_out, 26)
            for i in range(NT):
                tt(x[:, i, :], x[:, i, :], xT[:, 4 * i:4 * i + 4, :].rearrange("p c s -> p (c s)"),
                   ALU.add).then_inc(x_ready, 1)
            dve.wait_ge(x_ready, 4)
            tt(lbt[:, 0, :], vc("lb1"), vc("lb0"), ALU.subtract).then_inc(lb_diff, 1)
            v.memset(ones[:], 1.0).then_inc(zero_set, 1)
            for l in range(2):
                u, DO = FIRST2[l], 26 + 11 * l
                normalise(4 + 2 * l, 2 + 2 * l)
                gain_out(2 + 2 * l, f"n1_{l}")
                dve.wait_ge(dense_out, DO + 5)
                if l == 1:
                    dve.wait_ge(lb_sig, 2)
                    for d in range(2):
                        bound = lbt[:, 1, :].unsqueeze(2).to_broadcast([P, RH, S])
                        rest = lbt[:, 2, :].unsqueeze(2).to_broadcast([P, RH, S])
                        own.go(tt(k2[:, d], k2[:, d], rest, ALU.mult))
                        own.link(tt(decays[:, d], decays[:, d], rest, ALU.mult))
                        own.link(tt(decays[:, d], decays[:, d], bound, ALU.add))
                own.link(ts(qs, qs, RD ** -0.5, None, ALU.mult))
                own.go(tt(kdiag, k2[:, 0], k2[:, 1], ALU.add))
                own.go(tt(q2[:, 0], qs.rearrange("p h s -> p (h s)"), decays[:, 0].rearrange("p h s -> p (h s)"), ALU.mult))
                own.go(tt(q2[:, 1], qs.rearrange("p h s -> p (h s)"), decays[:, 1].rearrange("p h s -> p (h s)"), ALU.mult))
                own.settle()
                v.memset(stat[:, 7, 0:1], 0.0).then_inc(lv_ready, 1)

                def pick(n):
                    dve.wait_ge(lv_ps, 9 * l + n + 1)
                    for tl in range(NT):
                        src = WB[2 * (n % 2) + tl][:].rearrange("p (h t) -> p h t", h=RH)
                        if n == 0:
                            ins = v.tensor_copy(pairs[:, tl], src)
                        elif n == LEVELS:
                            ins = v.tensor_copy(cross[:, tl], src)
                        else:
                            m = masks[:, n:n + 1, :].to_broadcast([P, RH, P])
                            ins = v.copy_predicated(pairs[:, tl], m, src)
                        ins.then_inc(lv_sb, 1)
                    dve.wait_ge(lv_sb, 18 * l + 2 * n + 2)

                for n in range(2, LEVELS + 1):
                    dve.wait_ge(lv_ps, 9 * l + n)
                    half = 1 << (n - 2)
                    nb = RH * S // (2 * half)
                    M = 2 * nb
                    D0, D1 = DEC_AT[n - 2], DEC_AT[n - 1] if n < LEVELS else None
                    view = lambda at, dims: bass.AP(tensor=q2.tensor, offset=at, ap=[[WORK, P]] + dims)
                    qv = view(Q2_AT, [[RH * S + half, 2], [2 * half, nb], [1, half]])
                    kv = view(K2_AT, [[RH * S + half, 2], [2 * half, nb], [1, half]])
                    own.go(tt(qv, qv, view(D0 + 1, [[M - 1, 2], [2, nb], [0, half]]), ALU.mult))
                    own.go(tt(kv, kv, view(D0 + M + 1, [[-(M + 1), 2], [2, nb], [0, half]]), ALU.mult))
                    if n < LEVELS:
                        own.go(tt(view(D1, [[1, 2 * nb]]), view(D0, [[2, 2 * nb]]), view(D0 + 1, [[2, 2 * nb]]), ALU.mult))
                    own.settle()
                    v.memset(stat[:, 7, 0:1], 0.0).then_inc(lv_ready, 1)
                    dve.wait_ge(lv_ready, LEVELS * l + n)
                    if n == 2:
                        pick(0)
                    pick(n - 1)
                pick(LEVELS)
                dve.wait_ge(head_std, 2 * l + 1)
                own.link(v.reciprocal(stat[:, 4, 0:2], stat[:, 1, 0:2]))
                for j in range(NT):
                    ts(mix[:, j, 512:1024], WB[2 + j][:], stat[:, 4, j:j + 1], None, ALU.mult).then_inc(mix_tok, 1)
                dve.wait_ge(decay_in, 16 * (l + 1))
                for h in range(RH):
                    dve.wait_ge(rs_ps, RH * l + h + 1)
                    if h >= 2:
                        dve.wait_ge(rp_ps, RH * l + h - 1)
                    tt(rsc[h % 2], WB[h % 2][:].rearrange("p (i n) -> p i n", i=NT), decay[:, h], ALU.mult).then_inc(rs_sb, 1)
                dve.wait_ge(head_std, 2 * l + 2)
                own.link(v.reciprocal(stat[:, 3, :], stat[:, 3, :]))
                for j in range(NT):
                    tt(mix[:, j, 0:512].rearrange("p (h n) -> p h n", h=RH), DP[0][:, j, :].rearrange("p (h n) -> p h n", h=RH),
                       stat[:, 3, 4 * j:4 * j + 4].unsqueeze(2).to_broadcast([P, RH, P]), ALU.mult).then_inc(mix_tok, 1)
                for c in range(DC):
                    dve.wait_ge(gm_ps, 4 * l + c // 2 + 1)
                    gain, gate = (vc(f"ret_{l}", c), rgT) if c < RH else (vc(f"hgrn_{l}", c - RH), hgT)
                    stt(mT[:, c, :], WB[c // 2][:, (c % 2) * S:(c % 2 + 1) * S], gain, gate[:, c % RH, :], ALU.mult,
                        ALU.mult).then_inc(gm_sb, 1)
                dve.wait_ge(unit_done, MOE[l])
                for i in range(NT):
                    tt(x[:, i, :], x[:, i, :], DP[i][:].rearrange("p b n -> p (b n)"), ALU.add).then_inc(x_ready, 1)
                dve.wait_ge(x_ready, 6 + 6 * l)
                normalise(5 + 2 * l, 3 + 2 * l)
                gain_out(3 + 2 * l, f"n2_{l}")
                dve.wait_ge(lg_ps, l + 1)
                own.link(v.tensor_reduce(stat[:, 4, 0:2], WB[0][:, 0:NT * NE].rearrange("p (i e) -> p i e", i=NT), X, ALU.max))
                ts(stat[:, 5, 0:2], stat[:, 4, 0:2], -1.0, None, ALU.mult).then_inc(lg_max, 1)
                dve.wait_ge(lg_exp, 2 * (l + 1))
                own.link(v.reciprocal(stat[:, 6, 2:4], stat[:, 6, 0:2]))
                tt(aff, affe, stat[:, 6, 2:4].unsqueeze(2).to_broadcast([P, NT, NE]), ALU.mult).then_inc(aff_sb, 1)
                dve.wait_ge(aff_ps, l + 1)
                own.link(v.tensor_copy(affT, WB[1][0:NE, 0:S]))
                for _ in range(CAP // 8):
                    own.link(v.max(top8, affT))
                    own.link(v.match_replace(out=affT, in_to_replace=top8, in_values=affT, imm_value=-1.0))
                own.link(ts(selT, affT, 0.0, None, ALU.is_lt))
                own.link(v.tensor_tensor_scan(rankT, ones[0:NE].to_broadcast([NE, S]), selT, 0.0, ALU.mult, ALU.add))
                own.link(tt(rankT, rankT, selT, ALU.mult))
                ts(rankT, rankT, -1.0, None, ALU.add).then_inc(slot_sb, 1)
                own.go(v.memset(zeros, 0.0))
                dve.wait_ge(slot_ps, l + 1)
                own.link(v.tensor_copy(slot, WB[2][:, 0:NT * NE].rearrange("p (i e) -> p i e", i=NT)))
                for i in range(NT):
                    own.link(tt(chosen[:, i], slot[:, i, :].unsqueeze(2).to_broadcast([P, NE, CAP]),
                                cn("slots").unsqueeze(1).to_broadcast([P, NE, CAP]), ALU.is_equal))
                    tt(weighed[:, i], chosen[:, i], aff[:, i, :].unsqueeze(2).to_broadcast([P, NE, CAP]),
                       ALU.mult).then_inc(sel_ready, 1)
                g2 = vc(f"n2p_{l}").unsqueeze(2).to_broadcast([P, DC, CAP])
                with dve.Fori(0, NE) as e:
                    dve.wait_ge(ge_ps, e + ((NE + 1) * l + 2))
                    tt(xeT, WB[1][:, 0:256].rearrange("p (k c) -> p k c", k=DC), g2, ALU.mult).then_inc(xe_sb, 1)
                    dve.wait_ge(sg_sb, e + (NE * l + 1))
                    tt(hid.rearrange("p m b -> p (m b)"), sgate, WB[0][:, 256:512], ALU.mult).then_inc(hid_sb, 1)
                    dve.wait_ge(unit_done, e * 6 + (MOE[l] + 6))
                    v.tensor_copy(ye, WB[3][:, 0:256]).then_inc(ye_sb, 1)
                dve.wait_ge(sc_y, NE * (l + 1))
                for i in range(NT):
                    for b in range(2):
                        tt(x[:, i, 512 * b:512 * b + 512].rearrange("p (r n) -> p r n", r=2),
                           x[:, i, 512 * b:512 * b + 512].rearrange("p (r n) -> p r n", r=2),
                           DP[b][:, :, 256 * i:256 * i + 256], ALU.add).then_inc(x_ready, 1)
                dve.wait_ge(x_ready, 10 + 6 * l)
            dve.wait_ge(std_ready, 9)
            own.link(v.reciprocal(rstd[:], std[:]))
            dve.wait_ge(row_in, 48)
            for i in range(NT):
                stt(xs[:, i, :], x[:, i, :], rstd[:, i:i + 1], row[:], ALU.mult, ALU.mult).then_inc(final_done, 1)

        @block.tensor
        def _(pe):
            mm, tr = nc.tensor.matmul, nc.tensor.transpose

            def arrived(u):
                pe.wait_ge(landed[u % RING], 16 * (u // RING + 1))

            def token_unit(u, act_T, d):
                w = slot_of(u)
                nk = units[u][1]
                arrived(u)
                for i in range(NT):
                    for k in range(nk):
                        last = mm(d[:, i, :], act_T[:, k, i * P:(i + 1) * P], w[:, k, :], start=k == 0, stop=k == nk - 1)
                return last

            def t_unit(u, act_T, d):
                w = slot_of(u)
                nk = units[u][1]
                arrived(u)
                for c in range(4):
                    for k in range(nk):
                        last = mm(d[:, c // 2, (c % 2) * S:(c % 2 + 1) * S], w[:, k, c * P:(c + 1) * P],
                                  act_T[:, k, :], start=k == 0, stop=k == nk - 1)
                return last

            def rows_unit(u, act_T, first, last_unit):
                w = slot_of(u)
                arrived(u)
                for i in range(NT):
                    for n in range(2):
                        for k in range(4):
                            last = mm(DP[i][:, n, :], act_T[k][:, i * P:(i + 1) * P], w[:, k, 512 * n:512 * n + 512],
                                      start=first and k == 0, stop=last_unit and k == 3)
                return last

            def transpose_x(k):
                for b in range(4):
                    i, half = b // 2, b % 2
                    if half == 0:
                        pe.wait_ge(xs_ready, 2 * k + i + 1)
                    for c in range(4):
                        last = tr(WB[b][:, c * P:(c + 1) * P], xs[:, i, (4 * half + c) * P:(4 * half + c + 1) * P], ident)
                    last.then_inc(xt_ps, 1)

            pe.wait_ge(small_in, 32)
            transpose_x(0)
            pe.wait_ge(xT_ready, 4)

            def finish(ins):
                ins.then_inc(unit_done, 1)

            def bu(i):
                c, j = i // 4, i % 4
                if i >= 2:
                    pe.wait_ge(bu_used, i - 1)
                r = slice(32 * j, 32 * j + 32)
                for f in range(2):
                    last = mm(WB[i % 2][:, f * S:(f + 1) * S], bmat[r, c, f, :], uT[r, c, :], start=True, stop=True)
                last.then_inc(bu_ps, 1)

            def cy(i):
                c, j = i // 4, i % 4
                pe.wait_ge(state_ready, 2 * i + 2)
                if j == 0 and c >= 2:
                    pe.wait_ge(yd_ready, c - 1)
                o = WB[2 + c % 2][32 * j:32 * j + 32, 0:S]
                mm(o, ceff[:, 0, i, :], state[i % 2][:, 0, :], start=True, stop=False)
                mm(o, ceff[:, 1, i, :], state[i % 2][:, 1, :], start=False, stop=True).then_inc(y_ps, 1)

            finish(t_unit(0, xT, DP[0]))
            finish(t_unit(1, xT, DP[1]))
            pe.wait_ge(dense_out, 1)
            pe.wait_ge(bmat_in, 16)
            for m in range(2, 10):
                bu(2 * (m - 2))
                bu(2 * (m - 2) + 1)
                pe.wait_ge(dense_out, m - 1)
                finish((t_unit if m >= 8 else token_unit)(m, xT, DP[m % 2]))
                cy(2 * (m - 2))
                cy(2 * (m - 2) + 1)
            pe.wait_ge(dense_out, 9)
            pe.wait_ge(yg_ready, 4)
            finish(t_unit(10, yg, DP[0]))
            for b in range(8):
                src = q_tok if b < 4 else k_tok
                if b % 4 == 0:
                    pe.wait_ge(rope_done, 4 * (b // 4 + 1))
                if b >= 4:
                    pe.wait_ge(qk_sb, b - 3)
                for c in range(2):
                    for i in range(NT):
                        ch = 2 * (b % 4) + c
                        last = tr(WB[b % 4][:, (2 * c + i) * P:(2 * c + i + 1) * P], src[:, i, ch * P:(ch + 1) * P], ident)
                last.then_inc(qk_ps, 1)
            pe.wait_ge(qk_sb, 8)
            for h in range(HEADS + 2):
                if h < HEADS:
                    if h >= 2:
                        pe.wait_ge(sc_max, 2 * h - 2)
                    r, c = slice(64 * (h % 2), 64 * (h % 2) + 64), h // 2
                    mm(WB[h % 2][:, 0:P], qT[r, c, 0:P], kT[r, c, 0:P], start=True, stop=True)
                    mm(WB[h % 2][:, P:3 * P], qT[r, c, P:S], kT[r, c, :], start=True, stop=True).then_inc(sc_ps, 1)
                if 1 <= h <= HEADS:
                    g = h - 1
                    pe.wait_ge(sc_exp, 2 * g + 2)
                    if g >= 1:
                        pe.wait_ge(et_sb, g)
                    for k in range(3):
                        last = tr(WB[2][:, k * P:(k + 1) * P], esc[g % 2][:, k, :], ident)
                    last.then_inc(et_ps, 1)
                if h >= 2:
                    g = h - 2
                    pe.wait_ge(et_sb, g + 1)
                    if g % 4 == 0 and g >= 4:
                        pe.wait_ge(o_sb, 2 * (g // 4))
                    o = WB[3][:].rearrange("p (h i n) -> p h i n", h=4, i=NT)[:, g % 4]
                    e = escT[g % 2]
                    vh = v_tok[:, :, g * HD:(g + 1) * HD]
                    mm(o[:, 0, :], e[:, 0, :], vh[:, 0, :], start=True, stop=True)
                    mm(o[:, 1, :], e[:, 1, :], vh[:, 0, :], start=True, stop=False)
                    mm(o[:, 1, :], e[:, 2, :], vh[:, 1, :], start=False, stop=True).then_inc(pv_done, 1)
            pe.wait_ge(ssm_done, 1)
            pe.wait_ge(dense_out, 14)
            finish(rows_unit(11, [gsT[:, c, :] for c in range(4)], True, False))
            pe.wait_ge(o_sb, 8)
            for b in range(4):
                for c in range(2):
                    for i in range(NT):
                        ch = 2 * b + c
                        last = tr(WB[b][:, (2 * c + i) * P:(2 * c + i + 1) * P], att[:, i, ch * P:(ch + 1) * P], ident)
                last.then_inc(at_ps, 1)
            for n in range(2):
                pe.wait_ge(at_sb, 2 * n + 2)
                finish(rows_unit(12 + n, [mT0[:, 4 * n + c, :] for c in range(4)], False, n == 1))
            transpose_x(1)
            pe.wait_ge(xT_ready, 8)
            pe.wait_ge(dense_out, 16)
            pe.wait_ge(pool_in, 16)
            for g in range(4):
                if g >= 2:
                    pe.wait_ge(dense_out, 16 + g - 1)
                finish(token_unit(14 + g, xT, DP[g % 2]))
                pe.wait_ge(dense_out, 16 + g + 1)
                for b in range(2):
                    n = 2 * g + b
                    if n >= 4:
                        pe.wait_ge(mix_sb, n - 3)
                    for c in range(2):
                        ch = 4 * g + 2 * b + c
                        o = WB[n % 4][:, c * S:(c + 1) * S]
                        mm(o, u_tok[:, 0, ch * P:(ch + 1) * P], poolm[:, g, 0:S], start=True, stop=False)
                        last = mm(o[:, P:S], u_tok[:, 1, ch * P:(ch + 1) * P], poolm[:, g, S:3 * P], start=False,
                                  stop=True)
                    last.then_inc(mix_ps, 1)
            for g in range(4):
                pe.wait_ge(dense_out, 16 + 4 + g - 1)
                finish(t_unit(18 + g, xT, DP[g % 2]))
            for g in range(4):
                if g < 2:
                    pe.wait_ge(dense_out, 16 + 8 - 1 + g)
                else:
                    pe.wait_ge(gated, 4 * (g - 1))
                pe.wait_ge(mix_sb, 2 * g + 2)
                finish(t_unit(22 + g, mixT[:, 4 * g:4 * g + 4, :], DP[g % 2]))
            pe.wait_ge(gated, 16)
            for n in range(4):
                finish(rows_unit(26 + n, [gT[:, 4 * n + c, :] for c in range(4)], n == 0, n == 3))
            for l in range(2):
                u, DO = FIRST2[l], 26 + 11 * l
                transpose_x(2 + 2 * l)
                pe.wait_ge(xT_ready, 4 * (3 + 2 * l))

                def level(n):
                    pe.wait_ge(lv_ready, LEVELS * l + max(n, 1))
                    if n >= 2:
                        pe.wait_ge(lv_sb, 18 * l + 2 * (n - 1))
                    for tl in range(NT):
                        for h in range(RH):
                            o = WB[2 * (n % 2) + tl][:, h * P:(h + 1) * P]
                            here = slice(h * S + tl * P, h * S + (tl + 1) * P)
                            if n == 0:
                                last = mm(o, kdiag[:, h, tl * P:(tl + 1) * P], qs[:, h, tl * P:(tl + 1) * P],
                                          start=True, stop=True)
                            elif n == LEVELS:
                                t = 1 - tl
                                last = mm(o, k2[:, tl, h, tl * P:(tl + 1) * P],
                                          q2[:, t, h * S + t * P:h * S + (t + 1) * P], start=True, stop=True)
                            else:
                                half = 1 << (n - 1)
                                for d in range(2):
                                    last = mm(halves(o, half, d == 0), k2[:, d, h, tl * P:(tl + 1) * P],
                                              halves(q2[:, 1 - d, here], half, d == 0), start=True, stop=True)
                    last.then_inc(lv_ps, 1)

                out_so_far = (0, 1, 3, 5, 6, 7, 8, 9, 10)
                after = {3: (0, 1), 4: (2,), 5: (3,), 6: (4,), 7: (5, 6), 8: (7, 8)}
                for n in range(9):
                    if n >= 2:
                        pe.wait_ge(dense_out, DO + out_so_far[n - 1])
                    finish((token_unit if 3 <= n <= 6 else t_unit)(u + n, xT, DP[(u + n) % 2]))
                    for m in after.get(n, ()):
                        level(m)
                pe.wait_ge(lv_sb, 18 * (l + 1))
                for j in range(NT):
                    for h in range(RH):
                        o, c = WB[2 + j][:, h * P:(h + 1) * P], slice(h * P, (h + 1) * P)
                        mm(o, pairs[:, j, h, :], v2_tok[:, j, c], start=True, stop=False)
                        last = mm(o, cross[:, 1 - j, h, :], v2_tok[:, 1 - j, c], start=False, stop=True)
                last.then_inc(ho_ps, 1)
                pe.wait_ge(dense_out, DO + 11)
                pe.wait_ge(rot_done, 8 * (l + 1))
                for w, t in enumerate((rq_tok, rk_tok)):
                    for h in range(RH):
                        for i in range(NT):
                            at = (h % 2) * S + i * P
                            last = tr(DP[w][:, h // 2, at:at + P], t[:, i, h * P:(h + 1) * P], ident)
                    last.then_inc(rt_ps, 1)
                pe.wait_ge(rt_sb, 2 * (l + 1))
                for h in range(RH + 1):
                    if h < RH:
                        if h >= 2:
                            pe.wait_ge(rs_sb, RH * l + h - 1)
                        for i in range(NT):
                            last = mm(WB[h % 2][:, i * S:(i + 1) * S], rkT[:, h, i * P:(i + 1) * P], rqT[:, h, :],
                                      start=True, stop=True)
                        last.then_inc(rs_ps, 1)
                    if h >= 1:
                        g = h - 1
                        pe.wait_ge(rs_sb, RH * l + g + 1)
                        for j in range(NT):
                            for i in range(NT):
                                last = mm(DP[0][:, j, g * P:(g + 1) * P], rsc[g % 2][:, i, j * P:(j + 1) * P],
                                          rv_tok[:, i, g * P:(g + 1) * P], start=i == 0, stop=i == 1)
                        last.then_inc(rp_ps, 1)
                pe.wait_ge(mix_tok, 4 * (l + 1))
                for b in range(4):
                    for c in range(2):
                        for i in range(NT):
                            ch = 2 * b + c
                            last = tr(WB[b][:, (2 * c + i) * P:(2 * c + i + 1) * P], mix[:, i, ch * P:(ch + 1) * P], ident)
                    last.then_inc(gm_ps, 1)
                for n in range(2):
                    pe.wait_ge(gm_sb, 8 * l + 4 * (n + 1))
                    finish(rows_unit(OUT2[l] + n, [mT[:, 4 * n + c, :] for c in range(4)], n == 0, n == 1))
                transpose_x(3 + 2 * l)
                pe.wait_ge(xT_ready, 4 * (4 + 2 * l))
                pe.wait_ge(router_in, 32)
                for i in range(NT):
                    for k in range(DC):
                        last = mm(WB[0][:, NE * i:NE * i + NE], xT[:, k, i * P:(i + 1) * P], wr[:, l, k, :], start=k == 0,
                                  stop=k == DC - 1)
                last.then_inc(lg_ps, 1)
                pe.wait_ge(aff_sb, l + 1)
                for i in range(NT):
                    last = tr(WB[1][0:NE, i * P:(i + 1) * P], aff[:, i, :], ident)
                last.then_inc(aff_ps, 1)
                pe.wait_ge(slot_sb, l + 1)
                for i in range(NT):
                    last = tr(WB[2][:, NE * i:NE * i + NE], rankT[:, i * P:(i + 1) * P], ident[0:NE, 0:NE])
                last.then_inc(slot_ps, 1)
                pe.wait_ge(sel_ready, 2 * (l + 1))
                yb = [DP[r // 2][:, r % 2, :] for r in range(4)]
                for r in range(4):
                    last = mm(yb[r], zeros, chosen[:, 0].rearrange("p e c -> p (e c)"), start=True, stop=True)
                last.then_inc(ge_ps, 1)
                with pe.Fori(0, NE) as e:
                    one = e + (NE * l + 1)
                    pe.wait_ge(esel, e * 3 + (3 * NE * l + 3))
                    for k in range(DC):
                        for i in range(NT):
                            mm(WB[1][:, k * CAP:(k + 1) * CAP], xs[:, i, k:D:DC], csel[:, i, :], start=i == 0, stop=i == 1)
                    for i in range(NT):
                        last = tr(WB[1][:, 256 + i * P:256 + (i + 1) * P], wsel[:, i].rearrange("p q c -> p (q c)"), ident)
                    last.then_inc(ge_ps, 1)
                    pe.wait_ge(xe_sb, one)
                    for j in range(4):
                        s = (MOE[l] + j) % RING
                        pe.wait_ge(landed[s], e * 16 + 16 * ((MOE[l] + j) // RING + 1))
                        for k in range(4):
                            for q in range(4):
                                last = mm(WB[0][32 * q:32 * q + 32, 256 * (j % 2):256 * (j % 2) + 256],
                                          xeT[:, 4 * (j // 2) + k, :],
                                          ring[:, s, k * D + 256 * q:k * D + 256 * q + 256],
                                          start=j == 0 and k == 0, stop=j >= 2 and k == 3, skip_group_check=True)
                        last.then_inc(unit_done, 1)
                    pe.wait_ge(hid_sb, one)
                    for b in range(2):
                        last = tr(WB[2][:, b * P:(b + 1) * P], hid[:, :, b], ident)
                    last.then_inc(ht_ps, 1)
                    pe.wait_ge(ht_sb, one)
                    for j in range(2):
                        s = (MOE[l] + 4 + j) % RING
                        pe.wait_ge(landed[s], e * 16 + 16 * ((MOE[l] + 4 + j) // RING + 1))
                        for qq in range(2):
                            for b in range(2):
                                q = 2 * j + qq
                                for r in range(4):
                                    w = qq * 2 * FF + b * FF + 256 * r
                                    last = mm(WB[3][32 * r:32 * r + 32, 0:256], hidT[:, b, 32 * q:32 * q + 32],
                                              ring[:, s, w:w + 256], start=q == 0 and b == 0, stop=q == 3 and b == 1,
                                              skip_group_check=True)
                        last.then_inc(unit_done, 1)
                    pe.wait_ge(ye_sb, one)
                    pe.wait_ge(gt_sb, one)
                    for i in range(NT):
                        for r in range(4):
                            rows = slice(32 * r, 32 * r + 32)
                            last = mm(yb[r][:, 256 * i:256 * i + 256], wselT[rows, i, :], ye[rows, :], start=False,
                                      stop=False, skip_group_check=True)
                    last.then_inc(sc_y, 1)


_WEIGHTS = ["x", "post_norm", "even_w_in", "ssm_glu_w", "even_w_out", "odd_w_in", "pool_w", "odd_w_out", "w_in_2",
            "w_out_2", "w_router_2", "w_gate_2", "w_up_2", "w_down_2", "final_norm_g_2"]


def layout(inputs):
    g = {k: np.asarray(v) for k, v in inputs.items()}
    cols = lambda v: v.reshape(-1, P).T
    states = lambda v: v.reshape(SSM_TILES, P).T
    n2p = lambda v: v.reshape(P, DC)
    parts = {"pre0": cols(g["pre_norm"][0]), "pre1": cols(g["pre_norm"][1]),
             "pscale": cols(g["pool_scale"][0]), "glu_b": cols(g["ssm_glu_b"][0]), "ssm_d": cols(g["ssm_d"][0]),
             "lb0": cols(g["lower_bounds_2"][0]), "lb1": cols(g["lower_bounds_2"][1]),
             "a_re": states(g["ssm_a_re"][0]), "a_im": states(g["ssm_a_im"][0]),
             "log_dt": states(np.repeat(g["ssm_log_dt"][0], SSM_N))}
    for l in range(2):
        parts[f"n1_{l}"] = cols(g["norm1_g_2"][l])
        parts[f"n2_{l}"] = cols(g["norm2_g_2"][l])
        parts[f"n2p_{l}"] = n2p(g["norm2_g_2"][l])
        parts[f"ret_{l}"] = cols(g["ret_norm_g_2"][l])
        parts[f"hgrn_{l}"] = cols(g["hgrn_norm_g_2"][l])
    out = {n: np.ascontiguousarray(g[n]) for n in _WEIGHTS}
    out["vectors"] = np.ascontiguousarray(np.concatenate([parts[n] for n in VEC], axis=1))
    b = np.zeros((4, 4, 2, SSM_H, 2, 2, SSM_N), np.float32)
    c = np.zeros((2, SSM_N, 2, SSM_TILES, 2, SSM_H), np.float32)
    for f, (bn, cname) in enumerate((("ssm_b_re", "ssm_c_re"), ("ssm_b_im", "ssm_c_im"))):
        bb = g[bn][0].reshape(4, 4, 2, SSM_N, SSM_H)
        cc = g[cname][0].reshape(SSM_TILES, 2, SSM_H, SSM_N)
        for e in range(2):
            b[:, :, e, :, f, e, :] = bb[:, :, e].transpose(0, 1, 3, 2)
            c[e, :, f, :, e, :] = cc[:, e].transpose(2, 0, 1)
    out["ssm_b"] = np.ascontiguousarray(b.reshape(4, P, 2, P).transpose(1, 0, 2, 3).reshape(P, -1))
    out["ssm_c"] = c.reshape(P, -1)
    out["constants"], out["pool_mat"], out["decay"], out["pair_masks"] = constants()
    return out


def kernel(**inputs):
    import concourse.bacc as _bacc
    from concourse.bass_utils import run_bass_kernel_spmd as _run

    nc = _bacc.Bacc("TRN2", target_bir_lowering=False, num_devices=1)
    arrays, args = {}, {}
    for name, v in layout(inputs).items():
        arrays[f"in_{name}"] = v
        args[name] = nc.dram_tensor(f"in_{name}", v.shape, mybir.dt.from_np(v.dtype), kind="ExternalInput").ap()
    out = nc.dram_tensor("out", (1, S, D), F32, kind="ExternalOutput").ap()
    build(nc, args, out[0])
    r = _run(nc, [arrays], core_ids=[0])
    return r.results[0]["out"]
```
